# Optimizing a Trainium2 kernel written in Bass

```python
import jax, jax.numpy as jnp
from jax import lax
import numpy as np

D_MODEL = 1024
BATCH = 1
SEQ = 1024
DEPTH = 2

HEAD_DIM = 64
POOL_WIDTH = D_MODEL // 4
POOL_WINDOWS = (2, 4, 8, 16)
N_POOL_GROUPS = len(POOL_WINDOWS)
POOL_GC = POOL_WIDTH // N_POOL_GROUPS
ATTN_WIDTH = D_MODEL - POOL_WIDTH
N_ATTN_HEADS = ATTN_WIDTH // HEAD_DIM
DIL_PATTERNS = ((128, 1), (512, 4), (2048, 16))
HEADS_PER_PATTERN = N_ATTN_HEADS // len(DIL_PATTERNS)
ROT_DIM = HEAD_DIM // 4
ROPE_THETA = 500000.0
BLK = 128
D_FF = 4 * D_MODEL
PLE_DIM = 256
EPS = 1e-6


def rmsnorm(x, g):
    xf = x.astype(jnp.float32)
    y = xf * lax.rsqrt(jnp.mean(xf * xf, axis=-1, keepdims=True) + EPS)
    return (y * g.astype(jnp.float32)).astype(x.dtype)

def rotary_tables(positions, dtype):
    inv_freq = ROPE_THETA ** (-jnp.arange(0, ROT_DIM, 2, dtype=jnp.float32) / ROT_DIM)
    ang = positions.astype(jnp.float32)[..., None] * inv_freq
    return jnp.cos(ang)[:, :, None, :].astype(dtype), jnp.sin(ang)[:, :, None, :].astype(dtype)

def apply_partial_rotary(x, cos, sin):
    half = ROT_DIM // 2
    x1 = x[..., :half]
    x2 = x[..., half:ROT_DIM]
    rot = jnp.concatenate([x1 * cos - x2 * sin, x2 * cos + x1 * sin], axis=-1)
    return jnp.concatenate([rot, x[..., ROT_DIM:]], axis=-1)

def pool_mixer(u, w, scale):
    B, S, _ = u.shape
    ug = u.reshape(B, S, N_POOL_GROUPS, POOL_GC).astype(jnp.float32)
    c = lax.cumsum(ug, axis=1)
    c0 = jnp.pad(c, ((0, 0), (1, 0), (0, 0), (0, 0)))
    t = jnp.arange(S, dtype=jnp.int32)
    win = jnp.array(POOL_WINDOWS, dtype=jnp.int32)
    lo = jnp.maximum(t[:, None] + 1 - win[None, :], 0)
    c_lo = jnp.take_along_axis(c0, lo[None, :, :, None], axis=1)
    cnt = (t[:, None] + 1 - lo).astype(jnp.float32)
    y = ((c - c_lo) / cnt[None, :, :, None] - ug).astype(u.dtype)
    y = jnp.einsum('bsgc,gcd->bsgd', y, w).reshape(B, S, POOL_WIDTH)
    return y * scale

def dilated_window_attention(q, k, v, window, dil):
    B, S, H, Dh = q.shape
    steps = window // dil
    L = -(-S // (dil * BLK)) * BLK
    pad = L * dil - S
    nb = L // BLK

    def to_strided(a):
        a = jnp.pad(a, ((0, 0), (0, pad), (0, 0), (0, 0)))
        a = a.reshape(B, L, dil, H, Dh).transpose(0, 2, 1, 3, 4)
        return a.reshape(B, dil, nb, BLK, H, Dh)

    def with_prev(a):
        prev = jnp.pad(a[:, :, :-1], ((0, 0), (0, 0), (1, 0), (0, 0), (0, 0), (0, 0)))
        return jnp.concatenate([prev, a], axis=3)

    qs = to_strided(q)
    kb = with_prev(to_strided(k))
    vb = with_prev(to_strided(v))
    s = jnp.einsum('brnqhd,brnkhd->brnhqk', qs, kb,
                   preferred_element_type=jnp.float32) * (HEAD_DIM ** -0.5)
    qi = jnp.arange(nb)[:, None] * BLK + jnp.arange(BLK)[None, :]
    ki = jnp.arange(nb)[:, None] * BLK - BLK + jnp.arange(2 * BLK)[None, :]
    dist = qi[:, :, None] - ki[:, None, :]
    valid = (dist >= 0) & (dist <= steps) & (ki[:, None, :] >= 0)
    s = jnp.where(valid[None, None, :, None], s, -jnp.inf)
    m = jnp.max(s, axis=-1, keepdims=True)
    e = jnp.exp(s - m)
    l = jnp.sum(e, axis=-1, keepdims=True)
    o = jnp.einsum('brnhqk,brnkhd->brnqhd', e / l, vb.astype(jnp.float32))
    lse = (m + jnp.log(l))[..., 0]
    o = o.reshape(B, dil, L, H, Dh).transpose(0, 2, 1, 3, 4).reshape(B, L * dil, H, Dh)[:, :S]
    lse = lse.transpose(0, 1, 2, 4, 3).reshape(B, dil, L, H).transpose(0, 2, 1, 3)
    lse = lse.reshape(B, L * dil, H)[:, :S]
    return o, lse

def dilated_mixer(q, k, v):
    outs, lses = [], []
    for g, (window, dil) in enumerate(DIL_PATTERNS):
        sl = slice(g * HEADS_PER_PATTERN, (g + 1) * HEADS_PER_PATTERN)
        o, lse = dilated_window_attention(q[:, :, sl], k[:, :, sl], v[:, :, sl], window, dil)
        outs.append(o)
        lses.append(lse)
    wts = jax.nn.softmax(jnp.stack(lses, axis=0), axis=0)
    o = jnp.concatenate([outs[g] * wts[g][..., None] for g in range(len(DIL_PATTERNS))], axis=2)
    B, S = q.shape[0], q.shape[1]
    return o.reshape(B, S, ATTN_WIDTH).astype(q.dtype)

def first_inputs(seed: int = 0) -> dict:
    key = jax.random.key(seed)
    ks = jax.random.split(key, 16)
    f32 = jnp.float32
    n_in = POOL_WIDTH + 3 * ATTN_WIDTH
    return {
        "x": jax.random.normal(ks[0], (BATCH, SEQ, D_MODEL), f32),
        "p": jax.random.normal(ks[1], (DEPTH, BATCH, SEQ, PLE_DIM), f32),
        "positions": jnp.broadcast_to(jnp.arange(SEQ, dtype=jnp.int32), (BATCH, SEQ)),
        "norm1": 1.0 + 0.02 * jax.random.normal(ks[2], (DEPTH, D_MODEL), f32),
        "w_in": jax.random.normal(ks[3], (DEPTH, D_MODEL, n_in), f32) * D_MODEL ** -0.5,
        "pool_w": jax.random.normal(ks[4], (DEPTH, N_POOL_GROUPS, POOL_GC, POOL_GC), f32) * POOL_GC ** -0.5,
        "pool_scale": 1.0 + 0.02 * jax.random.normal(ks[5], (DEPTH, POOL_WIDTH), f32),
        "w_out": jax.random.normal(ks[6], (DEPTH, POOL_WIDTH + ATTN_WIDTH, D_MODEL), f32) * (POOL_WIDTH + ATTN_WIDTH) ** -0.5,
        "norm2": 1.0 + 0.02 * jax.random.normal(ks[7], (DEPTH, D_MODEL), f32),
        "w_up": jax.random.normal(ks[8], (DEPTH, D_MODEL, D_FF), f32) * D_MODEL ** -0.5,
        "w_down": jax.random.normal(ks[9], (DEPTH, D_FF, D_MODEL), f32) * D_FF ** -0.5,
        "norm3": 1.0 + 0.02 * jax.random.normal(ks[10], (DEPTH, D_MODEL), f32),
        "w_gate": jax.random.normal(ks[11], (DEPTH, D_MODEL, D_MODEL), f32) * D_MODEL ** -0.5,
        "w_ple": jax.random.normal(ks[12], (DEPTH, PLE_DIM, D_MODEL), f32) * PLE_DIM ** -0.5,
        "final_norm": 1.0 + 0.02 * jax.random.normal(ks[13], (D_MODEL,), f32),
    }

def first_block(x, p, positions, norm1, w_in, pool_w, pool_scale, w_out, norm2, w_up, w_down,
              norm3, w_gate, w_ple, final_norm):
    B, S, _ = x.shape
    cos, sin = rotary_tables(positions, x.dtype)
    h = x
    for i in range(DEPTH):
        hn = rmsnorm(h, norm1[i])
        z = hn @ w_in[i]
        u = z[..., :POOL_WIDTH]
        q, k, v = jnp.split(z[..., POOL_WIDTH:], 3, axis=-1)
        q = apply_partial_rotary(q.reshape(B, S, N_ATTN_HEADS, HEAD_DIM), cos, sin)
        k = apply_partial_rotary(k.reshape(B, S, N_ATTN_HEADS, HEAD_DIM), cos, sin)
        v = v.reshape(B, S, N_ATTN_HEADS, HEAD_DIM)
        pool_out = pool_mixer(u, pool_w[i], pool_scale[i])
        attn_out = dilated_mixer(q, k, v)
        h = h + jnp.concatenate([pool_out, attn_out], axis=-1) @ w_out[i]
        hn = rmsnorm(h, norm2[i])
        h = h + jnp.square(jax.nn.relu(hn @ w_up[i])) @ w_down[i]
        gate = jax.nn.sigmoid(rmsnorm(h, norm3[i]) @ w_gate[i])
        h = h + gate * (p[i] @ w_ple[i])
    return rmsnorm(h, final_norm)


DEPTH_2 = 1

ATT_HEAD_DIM = 64
D_ATT = D_MODEL // 2
N_ATT_HEADS = D_ATT // ATT_HEAD_DIM
D_CONV = D_MODEL // 2
N_CONV_GROUPS = 8
CONV_WIDTH = 31
Q_BLOCK = 128
LN_EPS = 1e-5
GATE_INIT_STD = 0.02
DEEPNORM_ALPHA = (2 * DEPTH_2) ** 0.25
DEEPNORM_BETA = (8 * DEPTH_2) ** -0.25
IN_WIDTHS = (D_ATT, D_ATT, D_ATT, D_ATT, D_CONV, D_CONV, D_CONV, D_MODEL, D_MODEL)
D_IN = sum(IN_WIDTHS)


def _split_points():
    pts, acc = [], 0
    for w in IN_WIDTHS[:-1]:
        acc += w
        pts.append(acc)
    return pts

def layer_norm(x, g, b):
    xf = x.astype(jnp.float32)
    mu = jnp.mean(xf, axis=-1, keepdims=True)
    var = jnp.mean(jnp.square(xf - mu), axis=-1, keepdims=True)
    return ((xf - mu) * lax.rsqrt(var + LN_EPS) * g + b).astype(x.dtype)

def stick_breaking_attention(q, k, v):
    S = q.shape[1]
    scale = ATT_HEAD_DIM ** -0.5
    outs = []
    for blk in range(S // Q_BLOCK):
        q0 = blk * Q_BLOCK
        q1 = q0 + Q_BLOCK
        qb = q[:, q0:q1]
        kb = k[:, :q1]
        vb = v[:, :q1]
        z = jnp.einsum('bthd,bshd->bhts', qb, kb).astype(jnp.float32) * scale
        t_pos = q0 + jnp.arange(Q_BLOCK)[:, None]
        s_pos = jnp.arange(q1)[None, :]
        causal = s_pos < t_pos
        log_fail = jnp.where(causal, jax.nn.log_sigmoid(-z), 0.0)
        later = lax.cumsum(log_fail, axis=3, reverse=True) - log_fail
        w = jnp.where(causal, jnp.exp(jax.nn.log_sigmoid(z) + later), 0.0)
        outs.append(jnp.einsum('bhts,bshd->bthd', w.astype(vb.dtype), vb))
    return jnp.concatenate(outs, axis=1)

def causal_depthwise_conv(u, w, b):
    C = u.shape[-1]
    up = jnp.pad(u, ((0, 0), (CONV_WIDTH - 1, 0), (0, 0)))
    out = lax.conv_general_dilated(up, w[:, None, :].astype(u.dtype), window_strides=(1,), padding='VALID',
                                   dimension_numbers=('NWC', 'WIO', 'NWC'), feature_group_count=C)
    return out + b

def hybrid_layer(x, w_in, b_in, conv_w, conv_b, conv_ln_g, conv_ln_b,
                 w_att_proj, w_conv_proj, b_conv_proj, w_out, ln_g, ln_b):
    B, S, _ = x.shape
    u = jnp.einsum('bsd,de->bse', x, w_in) + b_in
    q, k, v, z_att, glu_a, glu_b, z_conv, g_att, g_conv = jnp.split(u, _split_points(), axis=-1)

    heads = lambda t: t.reshape(B, S, N_ATT_HEADS, ATT_HEAD_DIM)
    att = stick_breaking_attention(heads(q), heads(k), heads(v)).reshape(B, S, D_ATT)
    att_branch = jnp.einsum('bsc,cd->bsd', att * jax.nn.silu(z_att), w_att_proj)

    c = glu_a * jax.nn.sigmoid(glu_b)
    c = causal_depthwise_conv(c, conv_w, conv_b)
    c = jax.nn.silu(layer_norm(c, conv_ln_g, conv_ln_b))
    conv_branch = jnp.einsum('bsc,cd->bsd', c * jax.nn.silu(z_conv), w_conv_proj) + b_conv_proj

    merged = jax.nn.sigmoid(g_att) * att_branch + jax.nn.sigmoid(g_conv) * conv_branch
    y = jnp.einsum('bsd,de->bse', merged, w_out)
    return layer_norm(DEEPNORM_ALPHA * x + y, ln_g, ln_b)

def second_inputs(seed: int = 0) -> dict:
    key = jax.random.key(seed)
    ks = jax.random.split(key, 13)
    L, D = DEPTH_2, D_MODEL
    nrm = lambda k, shape, s: jax.random.normal(k, shape, jnp.float32) * s
    x = nrm(ks[0], (BATCH, SEQ, D), 1.0)
    col_scale = jnp.ones((D_IN,), jnp.float32).at[2 * D_ATT:3 * D_ATT].set(DEEPNORM_BETA)
    w_in = nrm(ks[1], (L, D, D_IN), D ** -0.5) * col_scale
    b_in = nrm(ks[2], (L, D_IN), GATE_INIT_STD)
    conv_w = nrm(ks[3], (L, CONV_WIDTH, D_CONV), CONV_WIDTH ** -0.5)
    conv_b = nrm(ks[4], (L, D_CONV), GATE_INIT_STD)
    conv_ln_g = 1.0 + nrm(ks[5], (L, D_CONV), GATE_INIT_STD)
    conv_ln_b = nrm(ks[6], (L, D_CONV), GATE_INIT_STD)
    w_att_proj = nrm(ks[7], (L, D_ATT, D), D_ATT ** -0.5 * DEEPNORM_BETA)
    w_conv_proj = nrm(ks[8], (L, D_CONV, D), D_CONV ** -0.5 * DEEPNORM_BETA)
    b_conv_proj = nrm(ks[9], (L, D), GATE_INIT_STD)
    w_out = nrm(ks[10], (L, D, D), D ** -0.5 * DEEPNORM_BETA)
    ln_g = 1.0 + nrm(ks[11], (L, D), GATE_INIT_STD)
    ln_b = nrm(ks[12], (L, D), GATE_INIT_STD)
    return {'x': x, 'w_in': w_in, 'b_in': b_in, 'conv_w': conv_w, 'conv_b': conv_b,
            'conv_ln_g': conv_ln_g, 'conv_ln_b': conv_ln_b, 'w_att_proj': w_att_proj,
            'w_conv_proj': w_conv_proj, 'b_conv_proj': b_conv_proj, 'w_out': w_out,
            'ln_g': ln_g, 'ln_b': ln_b}

def second_block(x, w_in, b_in, conv_w, conv_b, conv_ln_g, conv_ln_b,
              w_att_proj, w_conv_proj, b_conv_proj, w_out, ln_g, ln_b):
    for l in range(DEPTH_2):
        x = hybrid_layer(x, w_in[l], b_in[l], conv_w[l], conv_b[l], conv_ln_g[l], conv_ln_b[l],
                         w_att_proj[l], w_conv_proj[l], b_conv_proj[l], w_out[l], ln_g[l], ln_b[l])
    return x


_first_inputs = second_inputs


def second_inputs(seed=0):
    import zlib

    import numpy as np

    out = dict(_first_inputs(seed))
    spreads = {}
    factors = {'b_in': 8.0,
     'conv_b': 8.0,
     'conv_ln_g': 8.0,
     'conv_ln_b': 8.0,
     'b_conv_proj': 8.0,
     'ln_g': 2.829,
     'ln_b': 2.887}
    for name, (base, spread) in spreads.items():
        noise = np.random.default_rng([zlib.crc32(name.encode()), seed]).standard_normal(out[name].shape)
        drawn = base * np.exp(spread * noise) if base else spread * noise
        out[name] = __import__('jax').numpy.asarray(drawn.astype(out[name].dtype))
    for name, factor in factors.items():
        out[name] = (out[name] * factor).astype(out[name].dtype)
    return out


_narrow_inputs = second_inputs


def second_inputs(seed=0):

    out = dict(_narrow_inputs(seed))
    wider = {'conv_ln_g': 6.31, 'conv_ln_b': 6.52, 'ln_g': 3.18, 'ln_b': 3.18}
    for name, times in wider.items():
        mean = out[name].mean()
        out[name] = (mean + times * (out[name] - mean)).astype(out[name].dtype)
    return out


def setup_inputs(seed=0):
    out = dict(first_inputs(seed))
    for name, value in second_inputs(seed + 1).items():
        if name != "x":
            out[name + "_2"] = value
    return out


def reference(
    x, p, positions, norm1, w_in, pool_w, pool_scale, w_out, norm2, w_up, w_down, norm3, w_gate,
    w_ple, final_norm, w_in_2, b_in_2, conv_w_2, conv_b_2, conv_ln_g_2, conv_ln_b_2,
    w_att_proj_2, w_conv_proj_2, b_conv_proj_2, w_out_2, ln_g_2, ln_b_2,
):
    x = first_block(
        x, p, positions, norm1, w_in, pool_w, pool_scale, w_out, norm2, w_up, w_down, norm3,
        w_gate, w_ple, final_norm,
    )
    return second_block(
        x, w_in_2, b_in_2, conv_w_2, conv_b_2, conv_ln_g_2, conv_ln_b_2, w_att_proj_2,
        w_conv_proj_2, b_conv_proj_2, w_out_2, ln_g_2, ln_b_2,
    )


_drawn_inputs = setup_inputs


def setup_inputs(seed=0):
    import zlib

    import numpy as np

    out = dict(_drawn_inputs(seed))
    spreads = {}
    factors = {'norm1': 4.762,
     'pool_scale': 5.034,
     'norm3': 200.0,
     'norm2': 8.0,
     'p': 4.289,
     'w_gate': 6.149,
     'w_ple': 4.282}
    for name, (base, spread) in spreads.items():
        noise = np.random.default_rng([zlib.crc32(name.encode()), seed]).standard_normal(out[name].shape)
        drawn = base * np.exp(spread * noise) if base else spread * noise
        out[name] = __import__('jax').numpy.asarray(drawn.astype(out[name].dtype))
    for name, factor in factors.items():
        out[name] = (out[name] * factor).astype(out[name].dtype)
    return out
```

```python
import math

import numpy as np

import concourse.bass as bass
from concourse import mybir

F32 = mybir.dt.float32
F32R = mybir.dt.float32r
I32 = mybir.dt.int32
ALU = mybir.AluOpType
ACT = mybir.ActivationFunctionType

P = 128
KC = 8
S = 1024
HALF = 512
ROUND = 12582912.0
TWO_PI = 2.0 * math.pi
PI_A = 6.28125
PI_B = float(np.float32(np.round((TWO_PI - PI_A) * 2 ** 20) / 2 ** 20))
PI_C = float(np.float32(TWO_PI - PI_A - PI_B))
BIG = 1.0e30

W_IN, W_OUT, FFN, GATE = 0, 20, 28, 92
PANELS = 108
BLOCKS = 4
HN1, CAT, HN2, HID, HN3, PLE = 0, 8, 16, 24, 56, 64
SOURCES = 66
COMBINE = 14
ROTARY_STEPS, FFN_STEPS = 24, 8
STEPS = ROTARY_STEPS + BLOCKS * FFN_STEPS
TABLE_SIN, TABLE_COS = 9, 11
UNITS = 32
GROUPS = 3


GLU, QKV, Z_ATT, G_ATT, Z_CONV, G_CONV, W_OUT2, PANELS2 = 0, 8, 20, 24, 40, 44, 60, 68
XN, ATT, CONV, MERGED = 0, 8, 12, 16
TAPS = 31
LN_MEAN1 = 3
LN_CENTRED1 = LN_MEAN1 + 2
LN_VAR1 = LN_MEAN1 + 5 + 4
LN_SCALED1 = LN_VAR1 + 2
SMALL = 9
CAP = 40.0

TILES = [(hd, half, kb, max(0, kb * P - half * HALF)) for hd in range(8) for half in range(2)
         for kb in range(4 * half + 3, -1, -1)]
DIAGONAL = [kb // 4 == half for _, half, kb, _ in TILES]
FIRST = [kb == 4 * half + 3 for _, half, kb, _ in TILES]
LAST = [kb == 0 for _, _, kb, _ in TILES]
GROUP = [2 * hd + half for hd, half, _, _ in TILES]


def in_pattern(x, g):
    if g == 1:
        return x.rearrange("p (n i r) -> p r n i", n=2, i=128, r=4)
    if g == 2:
        return x.rearrange("p (i r) -> p r i", i=64, r=16)
    return x


def like_pattern(x, g):
    if g == 1:
        return x.rearrange("p (r n i) -> p r n i", r=4, n=2, i=128)
    if g == 2:
        return x.rearrange("p (r i) -> p r i", r=16, i=64)
    return x


def has_prev(g, j):
    return (g == 0 and j > 0) or (g == 1 and j % 2 == 1)


def two_blocks(nc, x, p, positions, norm1, w_in, pool_w, pool_scale, w_out, norm2, w_up, w_down,
               norm3, w_gate, w_ple, final_norm, w_in_2, b_in_2, conv_w_2, conv_b_2, conv_ln_g_2,
               conv_ln_b_2, w_att_proj_2, w_conv_proj_2, b_conv_proj_2, w_out_2, ln_g_2, ln_b_2,
               rates, out):
    DEPTH = norm1.shape[0]
    X = KC
    N1, S1 = X + DEPTH * PANELS, DEPTH * SOURCES
    L1 = DEPTH * 3
    D = x.shape[2]
    SCALE = 64 ** -0.5
    ALPHA = 2 ** 0.25

    cursor = [-(-nc.sbuf_base // 64) * 64]

    def place(name, shape, dt=F32, at=None):
        size = 4 * int(np.prod(shape[1:]))
        offset = cursor[0] if at is None else at
        if at is None:
            cursor[0] += -(-size // 32) * 32
        return nc.alloc_sbuf_tensor_at(name, shape, dt, offset=offset)

    TILE = 4 * S
    at_h = cursor[0]
    h = place("h", [P, KC, S])
    at_P = cursor[0]
    P_hi = place("P_hi", [P, KC, S], F32R)
    P_lo = place("P_lo", [P, KC, S], F32R)
    at_Q = cursor[0]
    Q_hi = place("Q_hi", [P, KC, S], F32R)
    Q_lo = place("Q_lo", [P, KC, S], F32R)
    w_raw = place("w_raw", [P, 2, KC, P])
    w_hi = place("w_hi", [P, 2, KC, P], F32R)
    w_lo = place("w_lo", [P, 2, KC, P], F32R)
    at_rstd = cursor[0]
    rstd = place("rstd", [P, S])
    at_tmp = cursor[0]
    tmp = place("tmp", [P, S])
    at_rope = cursor[0]
    rope_c = place("rope_c", [P, S])
    rope_s = place("rope_s", [P, S])
    ident = place("ident", [P, P])
    ones = place("ones", [P, P])
    at_mask = cursor[0]
    mask = place("mask", [P, 2, P])
    mask_pair = place("mask_pair", [P, P])
    head_rows = place("head_rows", [P, 2, P])
    pool_bd = place("pool_bd", [P, 2, P])
    gains = place("gains", [P, 3, KC])
    pool_gain = place("pool_gain", [P, 2])
    final_gain = place("final_gain", [P, KC])
    rate = place("rate", [P, 1])
    small = place("small", [P, 8])
    first16 = place("first16", [P, 2, 16])
    row_max = place("row_max", [P, GROUPS, 8, 4])
    row_sum = place("row_sum", [P, GROUPS, 8, 4])
    neg_max = place("neg_max", [P, 2])
    bias2 = place("bias2", [P, 44])
    taps = place("taps", [P, 4, TAPS])
    conv_par = place("conv_par", [P, 3, 4])
    proj_bias = place("proj_bias", [P, KC])
    neg_mean = place("neg_mean", [P, 8])
    deviation = place("deviation", [P, 8])
    assert cursor[0] <= nc.sbuf_usable_end, (cursor[0], nc.sbuf_usable_end)

    qk = place("qk", [P, 4, S], at=at_Q)
    v_tok = place("v_tok", [P, 2, 8, P], at=at_Q + 4 * TILE)
    attn = place("attn", [P, 6, S], at=at_Q + 6 * TILE)
    pool_u = place("pool_u", [P, 2, S], at=at_Q + 12 * TILE)
    v_feat = place("v_feat", [P, 2, S], at=at_Q + 14 * TILE)
    mix = place("mix", [P, 2, S], at=at_Q + 14 * TILE)
    rows = place("rows", [P, 6, S], at=at_Q)
    sumsq_Q = place("sumsq_Q", [P, S], at=at_Q + 15 * TILE)
    p_raw = place("p_raw", [P, 8, 256], at=at_Q + 13 * TILE)
    x_raw = place("x_raw", [P, 8, D], at=at_P)
    sumsq_P = place("sumsq_P", [P, S], at=at_P + 15 * TILE)
    pos_int = place("pos_int", [P, S], I32, at=at_Q)
    pos = place("pos", [P, S], at=at_Q + TILE)
    ang = place("ang", [P, S], at=at_Q + 2 * TILE)
    turns = place("turns", [P, S], at=at_Q + 3 * TILE)

    p_feat = (tmp, rstd)

    q2 = place("q2", [P, 4, S], at=at_Q)
    k2 = place("k2", [P, 4, S], at=at_Q + 4 * TILE)
    v2 = place("v2", [P, 4, 8, P], at=at_Q + 8 * TILE)
    att2 = place("att2", [P, 4, S], at=at_Q + 12 * TILE)
    branch_hi = place("branch_hi", [P, 4, S], F32R, at=at_Q)
    branch_lo = place("branch_lo", [P, 4, S], F32R, at=at_Q + 4 * TILE)
    merged = place("merged", [P, KC, S], at=at_Q + 8 * TILE)
    merged_lo = place("merged_lo", [P, KC, S], F32R, at=at_Q)
    merged_hi = place("merged_hi", [P, KC, S], F32R, at=at_h)
    conv_in = place("conv_in", [P, 4, S], at=at_h)
    conv_out = place("conv_out", [P, 4, S], at=at_h + 4 * TILE)
    resid = place("resid", [P, 2, S], at=at_rope)
    y_tok = place("y_tok", [P, 8, D], at=at_Q + 8 * TILE)
    y_out = place("y_out", [P, 8, D], at=at_P)
    ln_gain = place("ln_gain", [P, D], at=at_tmp)
    ln_shift = place("ln_shift", [P, D], at=at_rstd)
    soft = place("soft", [P, 4, HALF], at=at_rope)
    stick = place("stick", [P, 2, HALF], at=at_tmp)
    later = place("later", [P, 2, HALF], at=at_rstd)
    v2_feat = place("v2_feat", [P, S], at=at_tmp)
    neg_tri = place("neg_tri", [P, P], at=at_mask)
    neg_ones = place("neg_ones", [P, P], at=at_mask + 4 * P)
    stat_sum = place("stat_sum", [P, S], at=at_rope)
    spare = place("spare", [P, S], at=at_rope + TILE)

    ring = [nc.alloc_psum_tensor(f"ring{i}", [P, S], F32) for i in range(2)]
    aux = [nc.alloc_psum_tensor(f"aux{i}", [P, S], F32) for i in range(2)]

    sem = nc.alloc_semaphore
    x_loaded = sem("x_loaded")
    const_loaded = sem("const_loaded")
    small_loaded = sem("small_loaded")
    gains_loaded = sem("gains_loaded")
    p_loaded = sem("p_loaded")
    raw_loaded = [sem("raw_loaded0"), sem("raw_loaded1")]
    out_stored = sem("out_stored")
    consts_made = sem("consts_made")
    w_hi_ready = sem("w_hi_ready")
    w_ready = sem("w_ready")
    mix_step = sem("mix_step")
    panel_done = sem("panel_done")
    stat_done = sem("stat_done")
    swapped = sem("swapped")
    v_turned = sem("v_turned")
    scored = sem("scored")
    probs_turned = sem("probs_turned")
    attended = sem("attended")
    rows_turned = sem("rows_turned")
    pooled = sem("pooled")
    weights_spread = sem("weights_spread")
    p_turned = sem("p_turned")
    p_taken = sem("p_taken")
    slot_free = sem("slot_free")
    table_step = sem("table_step")
    dve_step = sem("dve_step")
    summed = sem("summed")
    rstd_ready = sem("rstd_ready")
    rotated = sem("rotated")
    source_ready = sem("source_ready")
    cleared = sem("cleared")
    masked = sem("masked")
    max_ready = sem("max_ready")
    probs_taken = sem("probs_taken")
    dve_weighed = sem("dve_weighed")
    mix_done = sem("mix_done")
    combined = sem("combined")
    gated = sem("gated")
    sin_done = sem("sin_done")
    hi_ready = sem("hi_ready")
    squared = sem("squared")
    root_done = sem("root_done")
    v_taken = sem("v_taken")
    exped = sem("exped")
    attn_taken = sem("attn_taken")
    rows_taken = sem("rows_taken")
    shares_exped = sem("shares_exped")
    sigmoided = sem("sigmoided")

    normed = sem("normed")
    glued = sem("glued")
    convolved = sem("convolved")
    v2_taken = sem("v2_taken")
    v2_turned = sem("v2_turned")
    z_scored = sem("z_scored")
    z_summed = sem("z_summed")
    z_attended = sem("z_attended")
    z_capped = sem("z_capped")
    z_soft = sem("z_soft")
    z_later = sem("z_later")
    z_exped = sem("z_exped")
    z_logged = sem("z_logged")
    z_weighed = sem("z_weighed")
    z_soft_cut = sem("z_soft_cut")
    z_weight_cut = sem("z_weight_cut")
    z_taken = sem("z_taken")
    tri_made = sem("tri_made")
    branched = sem("branched")
    ln_step = sem("ln_step")
    ln_squared = sem("ln_squared")
    ln_silued = sem("ln_silued")
    ln_summed = sem("ln_summed")
    ln_root = sem("ln_root")
    merging = sem("merging")
    y_turned = sem("y_turned")
    y_taken = sem("y_taken")
    resid_done = sem("resid_done")
    ln_loaded = sem("ln_loaded")
    y_normed = sem("y_normed")
    y_squared = sem("y_squared")
    y_root = sem("y_root")
    y_done = sem("y_done")

    w_in_d = w_in.rearrange("l (k p) f -> l p k f", p=P)
    w_out_d = w_out.rearrange("l (k p) f -> l p k f", p=P)
    w_up_d = w_up.rearrange("l (k p) f -> l p k f", p=P)
    w_down_d = w_down.rearrange("l (b k p) f -> l b p k f", p=P, k=KC)
    w_gate_d = w_gate.rearrange("l (k p) f -> l p k f", p=P)
    w_ple_d = w_ple.rearrange("l (k p) f -> l p k f", p=P)
    p_d = p.rearrange("l o (t q) c -> l (o q) t c", q=P)
    x_d = x.rearrange("o (t q) d -> (o q) t d", q=P)
    pool_w_d = pool_w.rearrange("l (c e) i o -> l c e i o", e=2)

    from contextlib import ExitStack
    ctx = ExitStack()
    ctx.enter_context(nc.allow_non_contiguous_dma(reason="gains go to one feature per partition"))
    block = ctx.enter_context(nc.Block())

    @block.sync
    def _(sp):
        for t in range(8):
            sp.dma_start(x_raw[:, t], x_d[:, t]).then_inc(x_loaded, 16)
        sp.dma_start(pos_int[:], positions.partition_broadcast(P).rearrange("p o s -> p (o s)")).then_inc(const_loaded, 16)
        sp.dma_start(rate[:], rates).then_inc(const_loaded, 16)
        sp.dma_start(final_gain[:], final_norm.rearrange("(k q) -> q k", q=P)).then_inc(const_loaded, 16)

        small_loads = [(bias2[:], b_in_2[0].rearrange("(k q) -> q k", q=P)),
                       (conv_par[:, 0], conv_b_2[0].rearrange("(k q) -> q k", q=P)),
                       (conv_par[:, 1], conv_ln_g_2[0].rearrange("(k q) -> q k", q=P)),
                       (conv_par[:, 2], conv_ln_b_2[0].rearrange("(k q) -> q k", q=P)),
                       (proj_bias[:], b_conv_proj_2[0].rearrange("(k q) -> q k", q=P))]
        small_loads += [(taps[:, c], conv_w_2[0][:, c * P:c * P + P].rearrange("w q -> q w")) for c in range(4)]
        assert len(small_loads) == SMALL

        def panel(n, slot, src, kc=KC):
            sp.wait_ge(w_ready, n - X + 1)
            sp.dma_start(w_raw[:, slot, 0:kc], src).then_inc(raw_loaded[slot], 16)

        with sp.Fori(0, DEPTH) as l:
            N0 = X + l * PANELS
            sp.wait_ge(summed, l * 24 + 8)
            for i, norm in enumerate((norm1, norm2, norm3)):
                sp.dma_start(gains[:, i], norm[l].rearrange("(k q) -> q k", q=P)).then_inc(gains_loaded, 16)
            sp.dma_start(pool_gain[:], pool_scale[l].rearrange("(k q) -> q k", q=P)).then_inc(gains_loaded, 16)
            sp.wait_ge(consts_made, 1)
            for c in range(2):
                for e in range(2):
                    sp.dma_start(pool_bd[64 * e:64 * e + 64, c, 64 * e:64 * e + 64], pool_w_d[l][c, e]).then_inc(gains_loaded, 16)
            def exchange(f):
                g, i = (f - 2) // 6, (f - 2) % 6
                if f < 2 or i >= 4:
                    return
                if i == 0:
                    sp.wait_ge(slot_free, N0 + f + 1)
                else:
                    sp.wait_ge(rotated, l * 12 + 4 * g + i)
                for lo in (0, 64):
                    sp.dma_start(tmp[lo:lo + 8], qk[lo + 8:lo + 16, i]).then_inc(swapped, 16)
                    sp.dma_start(tmp[lo + 8:lo + 16], qk[lo:lo + 8, i]).then_inc(swapped, 16)

            for f in range(20):
                c = f if f < 2 else 2 + ((f - 2) % 6 // 2) * 6 + (f - 2) // 6 * 2 + f % 2
                panel(N0 + max(f - 1, 0), f % 2, w_in_d[l][:, :, c * P:(c + 1) * P])
                exchange(f - 3)
            for f in range(8):
                panel(N0 + W_OUT + f - 1, f % 2, w_out_d[l][:, :, f * P:(f + 1) * P])
                if f < 3:
                    exchange(W_OUT - 3 + f)
            with sp.Fori(0, BLOCKS - 1) as b:
                for f in range(8):
                    panel(N0 + b * 16 + (FFN + f - 1), f % 2, w_up_d[l][:, :, bass.ds(b * D + f * P, P)])
                for f in range(8):
                    panel(N0 + b * 16 + (FFN + 7 + f), f % 2, w_down_d[l][b][:, :, f * P:(f + 1) * P])
            for f in range(8):
                at = (BLOCKS - 1) * D + f * P
                panel(N0 + GATE - 17 + f, f % 2, w_up_d[l][:, :, at:at + P])
            for f in range(8):
                panel(N0 + GATE - 9 + f, f % 2, w_down_d[l][BLOCKS - 1][:, :, f * P:(f + 1) * P])
                if f == 2:
                    sp.wait_ge(panel_done, N0 + GATE - 8)
                    sp.dma_start(p_raw[:], p_d[l]).then_inc(p_loaded, 16)
            for f in range(8):
                panel(N0 + GATE + 2 * f - 1, 0, w_gate_d[l][:, :, f * P:(f + 1) * P])
                panel(N0 + GATE + 2 * f, 1, w_ple_d[l][:, :, f * P:(f + 1) * P], 2)

        for dst, src in small_loads:
            sp.dma_start(dst, src).then_inc(small_loaded, 16)
        w_in2_d = w_in_2[0].rearrange("(k q) f -> q k f", q=P)
        w_ap_d = w_att_proj_2[0].rearrange("(k q) f -> q k f", q=P)
        w_cp_d = w_conv_proj_2[0].rearrange("(k q) f -> q k f", q=P)
        w_out2_d = w_out_2[0].rearrange("(k q) f -> q k f", q=P)

        def panel2(m, src, f, kc=KC):
            panel(N1 + m - 1, m % 2, src[:, :, f * P:(f + 1) * P], kc)

        for f in range(4):
            panel2(GLU + 2 * f, w_in2_d, 16 + f)
            panel2(GLU + 2 * f + 1, w_in2_d, 20 + f)
        for f in range(12):
            panel2(QKV + f, w_in2_d, f)
        for f in range(4):
            panel2(Z_ATT + f, w_in2_d, 12 + f)
        for f in range(8):
            panel2(G_ATT + 2 * f, w_in2_d, 28 + f)
            panel2(G_ATT + 2 * f + 1, w_ap_d, f, 4)
        for f in range(4):
            panel2(Z_CONV + f, w_in2_d, 24 + f)
        for f in range(8):
            panel2(G_CONV + 2 * f, w_in2_d, 36 + f)
            panel2(G_CONV + 2 * f + 1, w_cp_d, f, 4)
        for f in range(8):
            panel2(W_OUT2 + f, w_out2_d, f)
        out_d = out.rearrange("o (t q) d -> (o q) t d", q=P)
        sp.wait_ge(merging, KC)
        for dst, src in ((ln_gain, ln_g_2), (ln_shift, ln_b_2)):
            sp.dma_start(dst[:], src.partition_broadcast(P).rearrange("p o d -> p (o d)")).then_inc(ln_loaded, 16)
        for t in range(8):
            sp.wait_ge(y_done, t + 1)
            sp.dma_start(out_d[:, t], y_out[:, t]).then_inc(out_stored, 16)
        sp.wait_ge(out_stored, 16 * KC)

    @block.gpsimd
    def _(pool):
        done, base = 0, 0

        def settled():
            nonlocal done
            done += 1
            pool.wait_ge(mix_step, base + done)

        g = nc.gpsimd
        g.memset(pool_bd[:], 0.0).then_inc(mix_step, 1)
        settled()
        g.memset(small[:, 3:4], 1e-5).then_inc(mix_step, 1)
        settled()
        g.memset(small[:, 0:1], 1e-6).then_inc(consts_made, 1)
        g.memset(ident[:], 0.0).then_inc(mix_step, 1)
        settled()
        g.affine_select(out=ident[:], in_=ident[:], compare_op=ALU.not_equal, fill=1.0, base=0, pattern=[[-1, P]], channel_multiplier=1).then_inc(mix_step, 1)
        settled()
        g.memset(ones[:], 1.0).then_inc(w_ready, 1)
        pool.wait_ge(w_ready, 1)
        g.memset(mask[:], 0.0).then_inc(mix_step, 1)
        settled()
        g.affine_select(out=mask[:, 0], in_=mask[:, 0], compare_op=ALU.is_ge, fill=-BIG, base=0, pattern=[[1, P]], channel_multiplier=-1).then_inc(mix_step, 1)
        settled()
        g.affine_select(out=mask[:, 1], in_=mask[:, 1], compare_op=ALU.is_ge, fill=-BIG, base=0, pattern=[[-1, P]], channel_multiplier=1).then_inc(mix_step, 1)
        settled()
        g.tensor_copy(mask_pair[:], mask[:, 1]).then_inc(mix_step, 1)
        settled()
        g.memset(mask_pair[64:128, 0:64], -BIG).then_inc(mix_step, 1)
        settled()
        g.memset(head_rows[:], 0.0).then_inc(mix_step, 1)
        settled()
        for i in range(2):
            g.affine_select(out=head_rows[:, i].rearrange("p (e m) -> p e m", e=2), in_=head_rows[:, i].rearrange("p (e m) -> p e m", e=2),
                                 compare_op=ALU.not_equal, fill=1.0, base=-2 * i, pattern=[[-1, 2], [0, 64]], channel_multiplier=1).then_inc(mix_step, 1)
            settled()
        for c in range(2):
            for e in range(2):
                w = (2, 4, 8, 16)[2 * c + e]
                g.memset(small[64 * e:64 * e + 64, 1 + c:2 + c], 1.0 / w).then_inc(mix_step, 1)
                settled()
                for t in range(16):
                    g.memset(first16[64 * e:64 * e + 64, c, t:t + 1], 1.0 / min(t + 1, w)).then_inc(mix_step, 1)
                    settled()
        g.memset(neg_max[:], 0.0).then_inc(consts_made, 1)
        before = done
        one = ones[:, 0:1].rearrange("p (a b) -> p a b", a=1)

        def split(n, used, nth, slot, kc=KC):
            pool.wait_ge(raw_loaded[slot], nth)
            pool.wait_ge(panel_done, used)
            g.tensor_tensor(w_hi[:, slot, 0:kc], w_raw[:, slot, 0:kc], one.broadcast_to([P, kc, P]), ALU.mult).then_inc(w_hi_ready, 1)
            pool.wait_ge(w_hi_ready, n - X + 1)
            g.tensor_tensor(w_lo[:, slot, 0:kc], w_raw[:, slot, 0:kc], w_hi[:, slot, 0:kc].bitcast(F32), ALU.subtract).then_inc(w_ready, 1)

        MIX = 19
        with pool.Fori(0, DEPTH) as l:
            N0, R0 = X + l * PANELS, l * (PANELS * 8)

            def layer_split(f, b=0, kc=KC):
                split(N0 + b * 16 + f, N0 + b * 16 + max(f - 1, 0), R0 + b * 128 + 16 * (f // 2 + 1), f % 2, kc)

            for f in range(10):
                layer_split(f)
            done, base = 0, before + l * MIX
            pool.wait_ge(slot_free, N0 + 2)
            pool.wait_ge(v_turned, l * 6 + 2)

            def window(dst, src, w, part=slice(0, P)):
                g.tensor_tensor(dst[part, 0:w], src[part, 0:w], ones[part, 0:w], ALU.mult).then_inc(mix_step, 1)
                settled()
                g.tensor_tensor(dst[part, w:S], src[part, w:S], src[part, 0:S - w], ALU.add).then_inc(mix_step, 1)
                settled()

            a, bb = mix[:, 0], mix[:, 1]
            top, low = slice(64, P), slice(0, 64)
            for c in range(2):
                window(a, pool_u[:, c], 1)
                if c == 1:
                    window(bb, a, 2)
                    window(a, bb, 4)
                window(bb, a, 2 if c == 0 else 8, top)
                g.tensor_tensor(bb[low, :], a[low, :], ones[low, 0:1].broadcast_to([64, S]), ALU.mult).then_inc(mix_step, 1)
                settled()
                g.tensor_tensor(a[:, 16:S], bb[:, 16:S], small[:, 1 + c:2 + c].broadcast_to([P, S - 16]), ALU.mult).then_inc(mix_step, 1)
                settled()
                g.tensor_tensor(a[:, 0:16], bb[:, 0:16], first16[:, c], ALU.mult).then_inc(mix_step, 1)
                settled()
                if c == 0:
                    g.tensor_tensor(pool_u[:, c], a, pool_u[:, c], ALU.subtract).then_inc(mix_step, 1)
                    settled()
                else:
                    g.tensor_tensor(pool_u[:, c], a, pool_u[:, c], ALU.subtract).then_inc(mix_done, 1)
            assert done == MIX
            for f in range(10, FFN):
                layer_split(f)
            with pool.Fori(0, BLOCKS) as b:
                for f in range(16):
                    layer_split(FFN + f, b)
            for f in range(8):
                layer_split(GATE + 2 * f)
                layer_split(GATE + 2 * f + 1, kc=2)

        def split2(m, kc=KC):
            split(N1 + m, N1 + m - 1, (N1 - X) * 8 + 16 * (m // 2 + 1), m % 2, kc)

        pool.wait_ge(attn_taken, DEPTH * GROUPS * UNITS // 2)
        g.memset(neg_tri[:], -1.0).then_inc(tri_made, 1)
        g.memset(neg_ones[:], -1.0).then_inc(tri_made, 1)
        pool.wait_ge(tri_made, 2)
        g.affine_select(out=neg_tri[:], in_=neg_tri[:], compare_op=ALU.is_ge, fill=0.0, base=0, pattern=[[-1, P]], channel_multiplier=1)\
            .then_inc(tri_made, 1)
        for m in range(Z_ATT):
            split2(m)
        d = 0
        for s in range(len(TILES) + 3):
            for i, buf, slots, cut in ((s - 1, soft, 4, z_soft_cut), (s - 2, stick, 2, z_weight_cut)):
                if 0 <= i < len(TILES) and DIAGONAL[i]:
                    pool.wait_ge(z_soft if buf is soft else z_weighed, i + 1)
                    o = buf[:, i % slots, TILES[i][3]:TILES[i][3] + P]
                    g.affine_select(out=o, in_=o, compare_op=ALU.is_ge, fill=0.0, base=-1, pattern=[[1, P]], channel_multiplier=-1)\
                        .then_inc(cut, 1)
        for m in range(Z_ATT, PANELS2):
            split2(m, 4 if (G_ATT <= m < Z_CONV or G_CONV <= m < W_OUT2) and m % 2 else KC)


    @block.tensor
    def _(pe):
        t = nc.tensor
        pe.wait_ge(consts_made, 2)

        def product(slot, src_hi, src_lo, kc, ready):
            for k in range(kc):
                pe.wait_ge(source_ready, ready + k + 1)
                for half in range(2):
                    cols = slice(half * HALF, half * HALF + HALF)
                    o = ring[slot][:, cols]
                    t.matmul(o, w_hi[:, slot, k], src_hi[:, k, cols], start=(k == 0), stop=False)
                    t.matmul(o, w_hi[:, slot, k], src_lo[:, k, cols], start=False, stop=False)
                    mm = t.matmul(o, w_lo[:, slot, k], src_hi[:, k, cols], start=False, stop=(k == kc - 1))
            return mm

        def panel(n, used, slot, src_hi, src_lo, ready, kc=KC):
            pe.wait_ge(w_ready, n - X + 2)
            pe.wait_ge(slot_free, used)
            product(slot, src_hi, src_lo, kc, ready).then_inc(panel_done, 1)

        def sum_squares(sumsq, n_summed):
            pe.wait_ge(summed, n_summed)
            for half in range(2):
                mm = t.matmul(aux[0][:, half * HALF:half * HALF + HALF], ones[:], sumsq[:, half * HALF:half * HALF + HALF], start=True, stop=True)
            mm.then_inc(stat_done, 1)

        pe.wait_ge(x_loaded, 16 * 8)
        for k in range(KC):
            if k >= 2:
                pe.wait_ge(slot_free, k - 1)
            for b in range(8):
                mm = t.transpose(ring[k % 2][:, b * P:b * P + P], x_raw[:, b, k * P:k * P + P], ident[:])
            mm.then_inc(panel_done, 1)
        pe.wait_ge(slot_free, KC)

        with pe.Fori(0, DEPTH) as l:
            N0, S0 = X + l * PANELS, l * SOURCES
            A0 = l * (GROUPS * UNITS)

            def layer_panel(f, src_hi, src_lo, source, b=0, kc=KC):
                panel(N0 + b * 16 + f, N0 + b * 16 + max(f - 1, 0), f % 2, src_hi, src_lo, S0 + (b * 8 if source == HID else 0) + source, kc)

            def turn_v(g, i):
                pe.wait_ge(slot_free, N0 + 2 + 6 * g + 4 + i + 1)
                if g or i:
                    pe.wait_ge(v_taken, l * 6 + 2 * g + i)
                if g:
                    pe.wait_ge(attn_taken, l * (GROUPS * UNITS // 2) + g * UNITS // 2)
                for j in range(8):
                    mm = t.transpose(aux[0][:, j * P:j * P + P], v_feat[:, i, j * P:j * P + P], ident[:])
                mm.then_inc(v_turned, 1)

            def attention(g):
                A = A0 + g * UNITS
                pe.wait_ge(slot_free, N0 + 2 + 6 * (g + 1))
                pe.wait_ge(rotated, l * 12 + 4 * g + 4)
                pe.wait_ge(v_taken, l * 6 + 2 * g + 2)
                for s in range(UNITS + 3):
                    if s < UNITS:
                        c, j, e = s // 16, s // 2 % 8, s % 2
                        rows_ = slice(64 * e, 64 * e + 64)
                        first = j - 1 if has_prev(g, j) else j
                        if s >= 2:
                            pe.wait_ge(masked, A + s - 1)
                        o = ring[0][:, HALF * (s % 2):HALF * (s % 2) + (j + 1 - first) * P]
                        t.matmul(o, qk[rows_, c, j * P:j * P + P], qk[rows_, 2 + c, first * P:(j + 1) * P],
                                 start=True, stop=True).then_inc(scored, 1)
                    u = s - 2
                    if 0 <= u < UNITS:
                        j = u // 2 % 8
                        pe.wait_ge(exped, A + u + 1)
                        if u >= 2:
                            pe.wait_ge(probs_taken, A + u - 1)
                        for b in range(2 if has_prev(g, j) else 1):
                            mm = t.transpose(ring[1][:, HALF * (u % 2) + b * P:HALF * (u % 2) + b * P + P],
                                             tmp[:, 256 * (u % 2) + b * P:256 * (u % 2) + b * P + P], ident[:])
                        mm.then_inc(probs_turned, 1)
                    u = s - 3
                    if 0 <= u < UNITS:
                        c, j, e = u // 16, u // 2 % 8, u % 2
                        rows_ = slice(64 * e, 64 * e + 64)
                        pe.wait_ge(probs_taken, A + u + 1)
                        pair = u // 2
                        if pair >= 2 and e == 0:
                            pe.wait_ge(attn_taken, l * (GROUPS * UNITS // 2) + g * (UNITS // 2) + pair - 1)
                        o = aux[0][rows_, HALF * (pair % 2):HALF * (pair % 2) + P]
                        blocks = (j - 1, j) if has_prev(g, j) else (j,)
                        for b, jj in enumerate(blocks):
                            mm = t.matmul(o, v_tok[:, c, jj, rows_], tmp[:, HALF + 256 * (u % 2) + b * P:HALF + 256 * (u % 2) + b * P + P],
                                          start=(b == 0), stop=(b == len(blocks) - 1))
                        mm.then_inc(attended, 1)

            sum_squares(sumsq_P, l * 24 + 8)
            for f in range(2):
                layer_panel(f, P_hi, P_lo, HN1)
            for g in range(GROUPS):
                for i in range(6):
                    layer_panel(2 + 6 * g + i, P_hi, P_lo, HN1)
                    if i == 5:
                        turn_v(g, 0)
                turn_v(g, 1)
                attention(g)

            pe.wait_ge(mix_done, l + 1)
            pe.wait_ge(gains_loaded, (l + 1) * (16 * 8))
            pe.wait_ge(masked, A0 + GROUPS * UNITS)
            pe.wait_ge(probs_taken, A0 + GROUPS * UNITS)
            for c in range(2):
                for half in range(2):
                    cols = slice(half * HALF, half * HALF + HALF)
                    mm = t.matmul(ring[c][:, cols], pool_bd[:, c], pool_u[:, c, cols], start=True, stop=True)
                mm.then_inc(pooled, 1)
            for i, where in enumerate((aux[0], aux[1], ring[0], ring[1], aux[0], aux[1])):
                if i == 0:
                    pe.wait_ge(attn_taken, (l + 1) * (GROUPS * UNITS // 2))
                    pe.wait_ge(exped, A0 + GROUPS * UNITS)
                if i in (2, 3):
                    pe.wait_ge(source_ready, S0 + CAT + i - 1)
                if i >= 4:
                    pe.wait_ge(rows_taken, l * 6 + i - 3)
                for j in range(8):
                    mm = t.transpose(where[0:4, j * P:j * P + P], (row_max if i < 3 else row_sum)[:, i % 3, j], ident[:])
                mm.then_inc(rows_turned, 1)
            for i in range(6):
                g = i // 2
                if i == 0:
                    pe.wait_ge(combined, l * COMBINE + COMBINE)
                    pe.wait_ge(rows_taken, (l + 1) * 6)
                if i >= 2:
                    pe.wait_ge(dve_weighed, l * 6 + i - 1)
                for half in range(2):
                    cols = slice(half * HALF, half * HALF + HALF)
                    mm = t.matmul(aux[i % 2][:, cols], head_rows[0:4, i % 2], rows[0:4, g, cols], start=True, stop=True)
                mm.then_inc(weights_spread, 1)

            for f in range(8):
                layer_panel(W_OUT + f, P_hi, P_lo, CAT)
            sum_squares(sumsq_Q, l * 24 + 16)
            def turn_p(c):
                if c == 0:
                    pe.wait_ge(p_loaded, (l + 1) * 16)
                else:
                    pe.wait_ge(p_taken, l * 2 + 1)
                for b in range(8):
                    mm = t.transpose(aux[0][:, b * P:b * P + P], p_raw[:, b, c * P:c * P + P], ident[:])
                mm.then_inc(p_turned, 1)

            with pe.Fori(0, BLOCKS - 1) as b:
                for f in range(8):
                    layer_panel(FFN + f, Q_hi, Q_lo, HN2, b)
                for f in range(8):
                    layer_panel(FFN + 8 + f, P_hi, P_lo, HID, b)
            for f in range(8):
                layer_panel(GATE - 16 + f, Q_hi, Q_lo, HN2)
            for f in range(8):
                layer_panel(GATE - 8 + f, P_hi, P_lo, HN3 - 8)
                if 1 <= f <= 2:
                    turn_p(f - 1)
            pe.wait_ge(p_taken, l * 2 + 2)
            sum_squares(sumsq_Q, l * 24 + 24)
            for f in range(8):
                layer_panel(GATE + 2 * f, Q_hi, Q_lo, HN3)
                layer_panel(GATE + 2 * f + 1, P_hi, P_lo, PLE, kc=2)

        def panel2(m, src_hi, src_lo, source, kc=KC):
            panel(N1 + m, N1 + m - 1, m % 2, src_hi, src_lo, S1 + source, kc)

        sum_squares(sumsq_P, 8 + 24 * DEPTH)
        for m in range(QKV):
            panel2(m, P_hi, P_lo, XN)

        def turn_v2(i):
            pe.wait_ge(slot_free, N1 + QKV + 8 + i + 1)
            if i >= 1:
                pe.wait_ge(v2_taken, i)
            for j in range(8):
                mm = t.transpose(aux[0][:, j * P:j * P + P], v2_feat[:, j * P:j * P + P], ident[:])
            mm.then_inc(v2_turned, 1)

        for i in range(12):
            panel2(QKV + i, P_hi, P_lo, XN)
            if i >= 9:
                turn_v2(i - 9)
        turn_v2(3)

        pe.wait_ge(tri_made, 3)
        pe.wait_ge(v2_taken, 4)

        def z_bank(i, col):
            return ring[i % 4 // 2][:, HALF * (i % 2) + col:HALF * (i % 2) + HALF]

        for s in range(len(TILES) + 3):
            i = s
            if i < len(TILES):
                hd, half, kb, col = TILES[i]
                e = slice(64 * (hd % 2), 64 * (hd % 2) + 64)
                if i >= 4:
                    pe.wait_ge(z_weighed, i - 3)
                t.matmul(z_bank(i, col), k2[e, hd // 2, kb * P:kb * P + P], q2[e, hd // 2, half * HALF + col:half * HALF + HALF],
                         start=True, stop=True).then_inc(z_scored, 1)
            i = s - 2
            if 0 <= i < len(TILES):
                hd, half, kb, col = TILES[i]
                if DIAGONAL[i]:
                    pe.wait_ge(z_soft_cut, sum(DIAGONAL[:i]) + 1)
                else:
                    pe.wait_ge(z_soft, i + 1)
                mm = t.matmul(z_bank(i, col), neg_tri[:], soft[:, i % 4, col:], start=False, stop=True, skip_group_check=True)
                if not FIRST[i]:
                    pe.wait_ge(z_later, sum(not x for x in LAST[:i]))
                    before = TILES[i - 1][3]
                    mm = t.matmul(z_bank(i, before), neg_ones[:], later[:, i % 2, before:], start=False, stop=True, skip_group_check=True)
                mm.then_inc(z_summed, 1)
            i = s - 3
            if 0 <= i < len(TILES):
                hd, half, kb, col = TILES[i]
                e = slice(64 * (hd % 2), 64 * (hd % 2) + 64)
                if DIAGONAL[i]:
                    pe.wait_ge(z_weight_cut, sum(DIAGONAL[:i]) + 1)
                else:
                    pe.wait_ge(z_weighed, i + 1)
                if FIRST[i] and GROUP[i] >= 2:
                    pe.wait_ge(z_taken, GROUP[i] - 1)
                t.matmul(aux[0][e, HALF * (GROUP[i] % 2) + col:HALF * (GROUP[i] % 2) + HALF], v2[:, hd // 2, kb, e], stick[:, i % 2, col:],
                         start=FIRST[i], stop=True, skip_group_check=True).then_inc(z_attended, 1)

        def ln_sum(src, n):
            pe.wait_ge(ln_step, n)
            for half in range(2):
                mm = t.matmul(aux[1][:, half * HALF:half * HALF + HALF], ones[:], src[:, half * HALF:half * HALF + HALF], start=True, stop=True)
            mm.then_inc(ln_summed, 1)

        for f in range(4):
            panel2(Z_ATT + f, P_hi, P_lo, XN)
        for f in range(8):
            panel2(G_ATT + 2 * f, P_hi, P_lo, XN)
            panel2(G_ATT + 2 * f + 1, branch_hi, branch_lo, ATT, 4)
            if f == 5:
                ln_sum(stat_sum, LN_MEAN1)
            if f == 7:
                ln_sum(stat_sum, LN_VAR1)
        for f in range(4):
            panel2(Z_CONV + f, P_hi, P_lo, XN)
        for f in range(8):
            panel2(G_CONV + 2 * f, P_hi, P_lo, XN)
            panel2(G_CONV + 2 * f + 1, branch_hi, branch_lo, CONV, 4)
        def turn_y(f):
            pe.wait_ge(resid_done, f + 1)
            if f >= 1:
                pe.wait_ge(y_taken, f)
            for b in range(8):
                chunk = resid[:, f % 2, b * P:b * P + P]
                t.transpose(aux[0][:, b * P:b * P + P], chunk, ident[:])
                mm = t.matmul(aux[1][:, b:b + 1], chunk, ones[:, 0:1], start=(f == 0 and b == 0), stop=(f == KC - 1), skip_group_check=True)
            mm.then_inc(y_turned, 1)

        for f in range(8):
            panel2(W_OUT2 + f, merged_hi, merged_lo, MERGED)
            if f >= 1:
                turn_y(f - 1)
        turn_y(7)

    @block.scalar
    def _(act):
        a = nc.scalar
        act.wait_ge(consts_made, 2)
        for i, table in enumerate((rope_s, rope_c)):
            act.wait_ge(table_step, TABLE_SIN if i == 0 else TABLE_COS)
            a.activation(table[:], (ang if i == 0 else turns)[:], ACT.Sin).then_inc(sin_done, 1)

        def square(k, read, n_summed):
            act.wait_ge(*read)
            if n_summed is not None:
                act.wait_ge(summed, n_summed)
            a.activation(aux[1][:], h[:, k], ACT.Square).then_inc(squared, 1)

        def root(n_stat, n_rstd):
            act.wait_ge(stat_done, n_stat)
            a.activation(rstd[:], aux[0][:], ACT.Sqrt, scale=1.0 / D, bias=small[:, 0:1]).then_inc(root_done, 1)

        for k in range(KC):
            square(k, (slot_free, k + 1), k or None)

        with act.Fori(0, DEPTH) as l:
            N0, S0 = X + l * PANELS, l * SOURCES
            A0 = l * (GROUPS * UNITS)

            def scaled(dst, gain):
                for k in range(KC):
                    a.activation(dst[:, k], h[:, k], ACT.Copy, scale=gain[:, k:k + 1]).then_inc(hi_ready, 1)

            act.wait_ge(gains_loaded, (l + 1) * (16 * 8))
            act.wait_ge(panel_done, N0)
            root(l * 3 + 1, l * 3)
            scaled(P_hi, gains[:, 0])
            for g in range(GROUPS):
                for i in range(2):
                    act.wait_ge(v_turned, l * 6 + 2 * g + i + 1)
                    if i == 0 and g > 0:
                        act.wait_ge(attended, A0 + g * UNITS)
                    a.activation(v_tok[:, i].rearrange("p j c -> p (j c)"), aux[0][:], ACT.Copy).then_inc(v_taken, 1)
                A = A0 + g * UNITS

                def take_outputs(pair):
                    c, j = pair // 8, pair % 8
                    act.wait_ge(attended, A + 2 * pair + 2)
                    dst = attn[:, 2 * g + c]
                    if g == 0:
                        dst = dst[:, j * P:j * P + P]
                    elif g == 1:
                        dst = in_pattern(dst, 1)[:, j // 2, j % 2]
                    else:
                        dst = in_pattern(dst, 2)[:, 2 * j:2 * j + 2]
                    src = aux[0][:, HALF * (pair % 2):HALF * (pair % 2) + P]
                    if g == 2:
                        src = src.rearrange("p (r i) -> p r i", r=2)
                    a.activation(dst, src, ACT.Copy).then_inc(attn_taken, 1)

                for u in range(UNITS):
                    c, j, e = u // 16, u // 2 % 8, u % 2
                    n = 2 * P if has_prev(g, j) else P
                    act.wait_ge(max_ready, A + u + 1)
                    x_ = tmp[:, 256 * (u % 2):256 * (u % 2) + n]
                    a.activation(x_, x_, ACT.Exp, scale=SCALE, bias=neg_max[:, u % 2:u % 2 + 1],
                                 accum_out=row_sum[:, g, j, 2 * c + e:2 * c + e + 1]).then_inc(exped, 1)
                    if u >= 5 and u % 2 == 1:
                        take_outputs((u - 5) // 2)
                take_outputs(14)
                take_outputs(15)

            act.wait_ge(panel_done, N0 + 20)
            for c in range(2):
                act.wait_ge(pooled, l * 2 + c + 1)
                a.activation(P_hi[:, c], ring[c][:], ACT.Copy, scale=pool_gain[:, c:c + 1]).then_inc(hi_ready, 1)
            for i, where in enumerate((aux[0], aux[1], ring[0], ring[1], aux[0], aux[1])):
                act.wait_ge(rows_turned, l * 6 + i + 1)
                g = i % 3
                src, dst = where[0:4, :], rows[0:4, i]
                src = like_pattern(src, g)
                a.activation(in_pattern(dst, g), src, ACT.Copy).then_inc(rows_taken, 1)
            for g in range(GROUPS):
                act.wait_ge(combined, l * COMBINE + 2 + g + 1)
                a.activation(rows[0:4, g], rows[0:4, g], ACT.Exp, scale=SCALE).then_inc(shares_exped, 1)
            for i in range(6):
                act.wait_ge(dve_weighed, l * 6 + i + 1)
                a.activation(P_hi[:, 2 + i], attn[:, i], ACT.Copy).then_inc(hi_ready, 1)
            def upper(dst, gain, f):
                a.activation(dst[:, f], h[:, f], ACT.Copy, scale=gain[:, f:f + 1]).then_inc(hi_ready, 1)

            for f in range(8):
                square(f, (slot_free, N0 + W_OUT + f + 1), l * 24 + 8 + f)
                upper(Q_hi, gains[:, 1], f)
            act.wait_ge(rstd_ready, l * 3 + 1)
            act.wait_ge(weights_spread, (l + 1) * 6)
            root(l * 3 + 2, l * 3 + 1)

            def hidden(b, f):
                act.wait_ge(dve_step, l * STEPS + ROTARY_STEPS + b * FFN_STEPS + f + 1)
                act.wait_ge(panel_done, N0 + b * 16 + (FFN + f + 1))
                a.activation(P_hi[:, f], tmp[:], ACT.Copy).then_inc(hi_ready, 1)

            with act.Fori(0, BLOCKS) as b:
                for f in range(8):
                    hidden(b, f)
            for f in range(8):
                square(f, (slot_free, N0 + GATE - 8 + f + 1), l * 24 + 16 + f)
                upper(Q_hi, gains[:, 2], f)
                if 1 <= f <= 2:
                    act.wait_ge(source_ready, S0 + HN3)
                    act.wait_ge(p_turned, l * 2 + f)
                    a.activation(p_feat[f - 1][:], aux[0][:], ACT.Copy).then_inc(p_taken, 1)
            act.wait_ge(panel_done, N0 + GATE)
            act.wait_ge(p_taken, (l + 1) * 2)
            for c in range(2):
                a.activation(P_hi[:, c], p_feat[c][:], ACT.Copy).then_inc(hi_ready, 1)
            act.wait_ge(source_ready, S0 + PLE + 2)
            root(l * 3 + 3, l * 3 + 2)
            for f in range(8):
                act.wait_ge(slot_free, N0 + GATE + 2 * f + 1)
                a.activation(tmp[:], tmp[:], ACT.Sigmoid).then_inc(sigmoided, 1)
                square(f, (gated, l * 8 + f + 1), l * 24 + 24 + f)

        act.wait_ge(gated, 8 * DEPTH)
        act.wait_ge(panel_done, N1)
        root(L1 + 1, L1)
        for k in range(KC):
            act.wait_ge(normed, k + 1)
            a.activation(P_hi[:, k], h[:, k], ACT.Copy).then_inc(hi_ready, 1)

        def gate(m, col, func):
            act.wait_ge(slot_free, N1 + m)
            act.wait_ge(panel_done, N1 + m + 1)
            a.activation(tmp[:], ring[m % 2][:], func, bias=bias2[:, col:col + 1]).then_inc(slot_free, 1)

        act.wait_ge(small_loaded, 16 * SMALL)
        for f in range(4):
            m = GLU + 2 * f + 1
            act.wait_ge(panel_done, N1 + m + 1)
            act.wait_ge(slot_free, N1 + m - 1)
            a.activation(tmp[:], ring[1][:], ACT.Sigmoid, bias=bias2[:, 20 + f:21 + f]).then_inc(glued, 1)
        for i in range(4):
            act.wait_ge(v2_turned, i + 1)
            a.activation(v2[:, i].rearrange("p j c -> p (j c)"), aux[0][:], ACT.Copy).then_inc(v2_taken, 1)

        def z_cols(i):
            return slice(HALF * (i % 2) + TILES[i][3], HALF * (i % 2) + HALF)

        a.preload_act_table_set("natural_log_exp_and_others")
        for s in range(len(TILES) + 4):
            i = s
            if i < len(TILES):
                x_ = soft[:, i % 4, TILES[i][3]:]
                act.wait_ge(z_capped, i + 1)
                a.activation(x_, x_, ACT.Exp).then_inc(z_exped, 1)
                act.wait_ge(z_exped, i + 1)
                a.activation(x_, x_, ACT.Ln, bias=1.0).then_inc(z_logged, 1)
            i = s - 2
            if 0 <= i < len(TILES):
                act.wait_ge(z_summed, i + 1)
                if i >= 2:
                    act.wait_ge(z_attended, i - 1)
                a.activation(stick[:, i % 2, TILES[i][3]:], ring[i % 4 // 2][:, z_cols(i)], ACT.Exp).then_inc(z_weighed, 1)
            i = s - 4
            if 0 <= i < len(TILES) and LAST[i]:
                hd, half, G = TILES[i][0], TILES[i][1], GROUP[i]
                e = slice(64 * (hd % 2), 64 * (hd % 2) + 64)
                act.wait_ge(z_attended, i + 1)
                a.activation(att2[e, hd // 2, half * HALF:half * HALF + HALF], aux[0][e, HALF * (G % 2):HALF * (G % 2) + HALF], ACT.Copy)\
                    .then_inc(z_taken, 1)

        def branch_high(f, source):
            act.wait_ge(branched, (f + 1) if source == ATT else 4 + f + 1)
            a.activation(branch_hi[:, f], (att2 if source == ATT else conv_out)[:, f], ACT.Copy).then_inc(hi_ready, 1)

        for f in range(4):
            gate(Z_ATT + f, 12 + f, ACT.Silu)
            branch_high(f, ATT)

        def ln_square(k, src, n):
            act.wait_ge(ln_step, n)
            a.activation(aux[1][:], src, ACT.Square).then_inc(ln_squared, 1)

        def ln_deviation(n, width):
            act.wait_ge(ln_summed, n)
            a.activation(rstd[:], aux[1][:], ACT.Sqrt, scale=1.0 / width, bias=small[:, 3:4]).then_inc(ln_root, 1)

        for f in range(8):
            gate(G_ATT + 2 * f, 28 + f, ACT.Sigmoid)
            if f == 7:
                for k in range(4):
                    ln_square(k, conv_out[:, k], LN_CENTRED1 + (3 + k if k else 0))
        ln_deviation(2, 512)
        for k in range(4):
            act.wait_ge(ln_step, LN_SCALED1 + k)
            a.activation(conv_out[:, k], conv_out[:, k], ACT.Silu, scale=conv_par[:, 1, k:k + 1], bias=conv_par[:, 2, k:k + 1]).then_inc(ln_silued, 1)
        for f in range(4):
            gate(Z_CONV + f, 24 + f, ACT.Silu)
            branch_high(f, CONV)
        for f in range(8):
            if f:
                act.wait_ge(merging, f)
            gate(G_CONV + 2 * f, 36 + f, ACT.Sigmoid)
        for k in range(KC):
            act.wait_ge(merging, k + 1)
            a.activation(merged_hi[:, k], merged[:, k], ACT.Copy).then_inc(hi_ready, 1)
        for f in range(KC):
            act.wait_ge(y_turned, f + 1)
            a.activation(y_tok[:, :, f * P:f * P + P], aux[0][:].rearrange("p (b c) -> p b c", b=8), ACT.Copy).then_inc(y_taken, 1)
        act.wait_ge(y_taken, KC)
        act.wait_ge(y_normed, 1)
        for b in range(8):
            if b >= 1:
                act.wait_ge(y_squared, b)
                a.activation(deviation[:, b - 1:b], deviation[:, b - 1:b], ACT.Sqrt, scale=1.0 / D, bias=small[:, 3:4]).then_inc(y_root, 1)
            a.activation(aux[0][:], y_tok[:, b], ACT.Square, bias=neg_mean[:, b:b + 1], accum_out=deviation[:, b:b + 1]).then_inc(y_squared, 1)
        act.wait_ge(y_squared, 8)
        a.activation(deviation[:, 7:8], deviation[:, 7:8], ACT.Sqrt, scale=1.0 / D, bias=small[:, 3:4]).then_inc(y_root, 1)

    @block.vector
    def _(dve):
        v = nc.vector
        at_table = 0

        def table_settled():
            nonlocal at_table
            at_table += 1
            dve.wait_ge(table_step, at_table)

        v.memset(tmp[:], 0.0).then_inc(table_step, 1)
        table_settled()
        dve.wait_ge(const_loaded, 16 * 3)
        v.tensor_copy(pos[:], pos_int[:]).then_inc(table_step, 1)
        table_settled()
        v.tensor_scalar(ang[:], pos[:], rate[:, 0:1], None, ALU.mult).then_inc(table_step, 1)
        table_settled()
        v.tensor_scalar(turns[:], ang[:], 1.0 / TWO_PI, ROUND, ALU.mult, ALU.add).then_inc(table_step, 1)
        table_settled()
        v.tensor_scalar(turns[:], turns[:], -ROUND, None, ALU.add).then_inc(table_step, 1)
        table_settled()
        for part in (PI_A, PI_B, PI_C):
            v.scalar_tensor_tensor(ang[:], turns[:], -part, ang[:], ALU.mult, ALU.add).then_inc(table_step, 1)
            table_settled()
        v.tensor_scalar(ang[:], ang[:], float(np.nextafter(np.float32(math.pi), np.float32(0))), -float(np.nextafter(np.float32(math.pi), np.float32(0))), ALU.min, ALU.max).then_inc(table_step, 1)
        table_settled()
        assert at_table == TABLE_SIN
        v.scalar_tensor_tensor(turns[:], ang[:], -1.0, ang[:], ALU.mult, ALU.max).then_inc(table_step, 1)
        table_settled()
        v.tensor_scalar(turns[:], turns[:], -1.0, math.pi / 2, ALU.mult, ALU.add).then_inc(table_step, 1)
        table_settled()
        assert at_table == TABLE_COS

        def add_squares(sumsq, f, n_squared, n_summed):
            dve.wait_ge(squared, n_squared)
            if f == 0:
                v.tensor_copy(sumsq[:], aux[1][:]).then_inc(summed, 1)
            else:
                dve.wait_ge(summed, n_summed)
                v.tensor_tensor(sumsq[:], aux[1][:], sumsq[:], ALU.add).then_inc(summed, 1)

        for k in range(KC):
            dve.wait_ge(panel_done, k + 1)
            v.tensor_copy(h[:, k], ring[k % 2][:]).then_inc(slot_free, 1)
            if k >= 1:
                add_squares(sumsq_P, k - 1, k, k - 1)
        add_squares(sumsq_P, 7, 8, 7)
        dve.wait_ge(sin_done, 2)
        dve.wait_ge(slot_free, KC)

        with dve.Fori(0, DEPTH) as l:
            N0, S0 = X + l * PANELS, l * SOURCES
            A0 = l * (GROUPS * UNITS)
            rotary = 0

            def lower(hi, lo, gain, source, k):
                dve.wait_ge(hi_ready, S0 + source + k + 1)
                v.scalar_tensor_tensor(lo[:, k], h[:, k], gain[:, k:k + 1], hi[:, k].bitcast(F32), ALU.mult, ALU.subtract)\
                    .then_inc(source_ready, 1)

            def invert_rms(n):
                dve.wait_ge(root_done, n)
                v.reciprocal(rstd[:], rstd[:]).then_inc(rstd_ready, 1)

            def low_part(lo, hi, src, source):
                dve.wait_ge(hi_ready, S0 + source + 1)
                v.tensor_tensor(lo, src, hi.bitcast(F32), ALU.subtract).then_inc(source_ready, 1)

            dve.wait_ge(gains_loaded, (l + 1) * (16 * 8))
            dve.wait_ge(panel_done, N0)
            dve.wait_ge(summed, l * 24 + 8)
            for k in range(KC):
                if k == KC - 1:
                    dve.wait_ge(stat_done, l * 3 + 1)
                lower(P_hi, P_lo, gains[:, 0], HN1, k)
            invert_rms(l * 3 + 1)
            for f in range(2):
                dve.wait_ge(rstd_ready, l * 3 + 1)
                dve.wait_ge(panel_done, N0 + f + 1)
                v.tensor_tensor(pool_u[:, f], ring[f][:], rstd[:], ALU.mult).then_inc(slot_free, 1)
            for g in range(GROUPS):
                if g == 1:
                    dve.wait_ge(mix_done, l + 1)
                for i in range(6):
                    n = 2 + 6 * g + i
                    dve.wait_ge(panel_done, N0 + n + 1)
                    dst = qk[:, i] if i < 4 else v_feat[:, i - 4]
                    v.tensor_tensor(like_pattern(dst, g), in_pattern(ring[n % 2][:], g), in_pattern(rstd[:], g), ALU.mult)\
                        .then_inc(slot_free, 1)
                    if 1 <= i <= 4:
                        c = i - 1
                        dve.wait_ge(swapped, l * (12 * 64) + (4 * g + c + 1) * 64)
                        v.tensor_tensor(like_pattern(tmp[:], g), like_pattern(tmp[:], g), in_pattern(rope_s[:], g), ALU.mult)\
                            .then_inc(dve_step, 1)
                        v.tensor_tensor(like_pattern(qk[:, c], g), like_pattern(qk[:, c], g), in_pattern(rope_c[:], g), ALU.mult)\
                            .then_inc(dve_step, 1)
                        rotary += 2
                        dve.wait_ge(dve_step, l * STEPS + rotary)
                        v.tensor_tensor(qk[:, c], qk[:, c], tmp[:], ALU.add).then_inc(rotated, 1)
                A = A0 + g * UNITS
                dve.wait_ge(rotated, l * 12 + 4 * g + 4)

                def take_probs(u):
                    n = 2 * P if has_prev(g, u // 2 % 8) else P
                    dve.wait_ge(probs_turned, A + u + 1)
                    if u >= 2:
                        dve.wait_ge(attended, A + u - 1)
                    v.tensor_copy(tmp[:, HALF + 256 * (u % 2):HALF + 256 * (u % 2) + n], ring[1][:, HALF * (u % 2):HALF * (u % 2) + n])\
                        .then_inc(probs_taken, 1)

                for u in range(UNITS):
                    c, j, e = u // 16, u // 2 % 8, u % 2
                    col = row_max[:, g, j, 2 * c + e:2 * c + e + 1]
                    n = 2 * P if has_prev(g, j) else P
                    m = mask[:].rearrange("p b k -> p (b k)")[:, 2 * P - n:2 * P] if g < 2 else mask_pair[:]
                    if u >= 2:
                        take_probs(u - 2)
                    else:
                        dve.wait_ge(scored, A + u + 1)
                        v.memset(neg_max[:, u:u + 1], 0.0).then_inc(cleared, 1)
                    v.tensor_tensor_reduce(out=tmp[:, 256 * (u % 2):256 * (u % 2) + n], in0=ring[0][:, HALF * (u % 2):HALF * (u % 2) + n],
                                           in1=m, scale=1.0, scalar=-3.0e38, op0=ALU.add, op1=ALU.max, accum_out=col).then_inc(masked, 1)
                    dve.wait_ge(masked, A + u + 1)
                    v.tensor_scalar(neg_max[:, u % 2:u % 2 + 1], col, -SCALE, None, ALU.mult).then_inc(max_ready, 1)
                take_probs(UNITS - 2)
                take_probs(UNITS - 1)

            dve.wait_ge(panel_done, N0 + 20)
            for c in range(2):
                dve.wait_ge(hi_ready, S0 + CAT + c + 1)
                v.scalar_tensor_tensor(P_lo[:, c], ring[c][:], pool_gain[:, c:c + 1], P_hi[:, c].bitcast(F32), ALU.mult, ALU.subtract)\
                    .then_inc(source_ready, 1)
            C0 = l * COMBINE
            r = [rows[0:4, i] for i in range(6)]
            top = rstd[0:4, :]
            dve.wait_ge(rows_taken, l * 6 + 3)
            v.tensor_tensor(top, r[0], r[1], ALU.max).then_inc(combined, 1)
            dve.wait_ge(combined, C0 + 1)
            v.tensor_tensor(top, top, r[2], ALU.max).then_inc(combined, 1)
            dve.wait_ge(combined, C0 + 2)
            for g in range(GROUPS):
                v.tensor_tensor(r[g], r[g], top, ALU.subtract).then_inc(combined, 1)
            for g in range(GROUPS):
                dve.wait_ge(shares_exped, l * 3 + g + 1)
                dve.wait_ge(rows_taken, l * 6 + 3 + g + 1)
                v.tensor_tensor(r[3 + g], r[3 + g], r[g], ALU.mult).then_inc(combined, 1)
            dve.wait_ge(combined, C0 + 2 + 2 * GROUPS)
            v.tensor_tensor(r[3], r[3], r[4], ALU.add).then_inc(combined, 1)
            dve.wait_ge(combined, C0 + 3 + 2 * GROUPS)
            v.tensor_tensor(r[3], r[3], r[5], ALU.add).then_inc(combined, 1)
            dve.wait_ge(combined, C0 + 4 + 2 * GROUPS)
            v.reciprocal(r[3], r[3]).then_inc(combined, 1)
            dve.wait_ge(combined, C0 + 5 + 2 * GROUPS)
            for g in range(GROUPS):
                v.tensor_tensor(r[g], r[g], r[3], ALU.mult).then_inc(combined, 1)
            for i in range(6):
                dve.wait_ge(weights_spread, l * 6 + i + 1)
                v.tensor_tensor(attn[:, i], aux[i % 2][:], attn[:, i], ALU.mult).then_inc(dve_weighed, 1)
                if i >= 1:
                    low_part(P_lo[:, 1 + i], P_hi[:, 1 + i], attn[:, i - 1], CAT + 1 + i)
            low_part(P_lo[:, 7], P_hi[:, 7], attn[:, 5], CAT + 7)

            def residual(n, f):
                dve.wait_ge(panel_done, n + 1)
                v.tensor_tensor(h[:, f], ring[f % 2][:], h[:, f], ALU.add).then_inc(slot_free, 1)

            for f in range(8):
                residual(N0 + W_OUT + f, f)
                if f >= 1:
                    add_squares(sumsq_Q, f - 1, l * 24 + 8 + f, l * 24 + 8 + f - 1)
                    lower(Q_hi, Q_lo, gains[:, 1], HN2, f - 1)
            add_squares(sumsq_Q, 7, l * 24 + 16, l * 24 + 15)
            dve.wait_ge(stat_done, l * 3 + 2)
            lower(Q_hi, Q_lo, gains[:, 1], HN2, 7)
            invert_rms(l * 3 + 2)
            assert rotary == ROTARY_STEPS

            def up(b, f):
                dve.wait_ge(rstd_ready, l * 3 + 2)
                dve.wait_ge(panel_done, N0 + b * 16 + (FFN + f + 1))
                v.scalar_tensor_tensor(tmp[:], ring[f % 2][:], 0.0, rstd[:], ALU.max, ALU.mult).then_inc(slot_free, 1)
                dve.wait_ge(slot_free, N0 + b * 16 + (FFN + f + 1))
                at = l * STEPS + ROTARY_STEPS + b * FFN_STEPS
                v.tensor_tensor(tmp[:], tmp[:], tmp[:], ALU.mult).then_inc(dve_step, 1)
                dve.wait_ge(dve_step, at + f + 1)
                dve.wait_ge(hi_ready, S0 + b * 8 + (HID + f + 1))
                v.tensor_tensor(P_lo[:, f], tmp[:], P_hi[:, f].bitcast(F32), ALU.subtract).then_inc(source_ready, 1)
                dve.wait_ge(source_ready, S0 + b * 8 + (HID + f + 1))

            with dve.Fori(0, BLOCKS - 1) as b:
                for f in range(8):
                    up(b, f)
                for f in range(8):
                    residual(N0 + b * 16 + (FFN + 8 + f), f)
                dve.wait_ge(slot_free, N0 + b * 16 + (FFN + 16))
            for f in range(8):
                up(BLOCKS - 1, f)
            for f in range(8):
                residual(N0 + (GATE - 8 + f), f)
                if f == 5:
                    dve.wait_ge(p_turned, (l + 1) * 2)
                if f >= 1:
                    add_squares(sumsq_Q, f - 1, l * 24 + 16 + f, l * 24 + 16 + f - 1)
                    lower(Q_hi, Q_lo, gains[:, 2], HN3, f - 1)
            add_squares(sumsq_Q, 7, l * 24 + 24, l * 24 + 23)
            dve.wait_ge(stat_done, l * 3 + 3)
            lower(Q_hi, Q_lo, gains[:, 2], HN3, 7)
            for c in range(2):
                low_part(P_lo[:, c], P_hi[:, c], p_feat[c][:], PLE + c)
            invert_rms(l * 3 + 3)
            for f in range(8):
                dve.wait_ge(rstd_ready, l * 3 + 3)
                dve.wait_ge(panel_done, N0 + GATE + 2 * f + 1)
                if f >= 1:
                    dve.wait_ge(gated, l * 8 + f)
                v.tensor_tensor(tmp[:], ring[0][:], rstd[:], ALU.mult).then_inc(slot_free, 1)
                dve.wait_ge(sigmoided, l * 8 + f + 1)
                dve.wait_ge(panel_done, N0 + GATE + 2 * f + 2)
                v.tensor_tensor(tmp[:], ring[1][:], tmp[:], ALU.mult).then_inc(slot_free, 1)
                dve.wait_ge(slot_free, N0 + GATE + 2 * f + 2)
                v.tensor_tensor(h[:, f], h[:, f], tmp[:], ALU.add).then_inc(gated, 1)
                if f >= 1:
                    add_squares(sumsq_P, f - 1, l * 24 + 24 + f, l * 24 + 24 + f - 1)
            add_squares(sumsq_P, 7, l * 24 + 32, l * 24 + 31)

        dve.wait_ge(const_loaded, 16 * 3)
        dve.wait_ge(gated, 8 * DEPTH)
        invert_rms(L1 + 1)
        dve.wait_ge(rstd_ready, L1 + 1)

        def low_part2(lo, hi, src, source):
            dve.wait_ge(hi_ready, S1 + source + 1)
            v.tensor_tensor(lo, src, hi.bitcast(F32), ALU.subtract).then_inc(source_ready, 1)

        for k in range(KC):
            v.scalar_tensor_tensor(h[:, k], h[:, k], final_gain[:, k:k + 1], rstd[:], ALU.mult, ALU.mult).then_inc(normed, 1)
            if k >= 1:
                dve.wait_ge(normed, k)
                low_part2(P_lo[:, k - 1], P_hi[:, k - 1], h[:, k - 1], XN + k - 1)
        dve.wait_ge(normed, KC)
        dve.wait_ge(stat_done, L1 + 1)
        low_part2(P_lo[:, 7], P_hi[:, 7], h[:, 7], XN + 7)

        dve.wait_ge(small_loaded, 16 * SMALL)
        dve.wait_ge(source_ready, S1 + 8)
        for f in range(4):
            dve.wait_ge(panel_done, N1 + GLU + 2 * f + 1)
            v.tensor_scalar(conv_in[:, f], ring[0][:], bias2[:, 16 + f:17 + f], None, ALU.add).then_inc(slot_free, 1)
            dve.wait_ge(slot_free, N1 + GLU + 2 * f + 1)
            dve.wait_ge(glued, f + 1)
            v.tensor_tensor(conv_in[:, f], conv_in[:, f], tmp[:], ALU.mult).then_inc(slot_free, 1)

        dve.wait_ge(slot_free, N1 + QKV)
        todo = [(w, c) for w in range(TAPS - 1, -1, -1) for c in range(4)]

        taken = 0

        def convolve(n):
            nonlocal taken
            for w, c in todo[taken:taken + n]:
                tap, shift = taps[:, c, w:w + 1], TAPS - 1 - w
                if shift == 0:
                    v.tensor_scalar(conv_out[:, c], conv_in[:, c], tap, conv_par[:, 0, c:c + 1], ALU.mult, ALU.add)\
                        .then_inc(convolved, 1)
                else:
                    dve.wait_ge(convolved, taken - 3)
                    v.scalar_tensor_tensor(conv_out[:, c, shift:], conv_in[:, c, 0:S - shift], tap, conv_out[:, c, shift:], ALU.mult, ALU.add)\
                        .then_inc(convolved, 1)
                taken += 1

        for i in range(12):
            dve.wait_ge(panel_done, N1 + QKV + i + 1)
            if i < 8:
                dst = (q2 if i < 4 else k2)[:, i % 4]
                v.tensor_scalar(dst, ring[i % 2][:], bias2[:, i:i + 1], SCALE if i < 4 else 1.0, ALU.add, ALU.mult).then_inc(slot_free, 1)
            else:
                if i > 8:
                    dve.wait_ge(v2_turned, i - 8)
                v.tensor_scalar(v2_feat[:], ring[i % 2][:], bias2[:, i:i + 1], None, ALU.add).then_inc(slot_free, 1)
            convolve(7)
        dve.wait_ge(slot_free, N1 + Z_ATT)

        def later_before(i):
            return sum(not x for x in LAST[:i])

        for s in range(len(TILES) + 2):
            i = s
            if i < len(TILES):
                dve.wait_ge(z_scored, i + 1)
                if i >= 4:
                    dve.wait_ge(z_summed, i - 3)
                    dve.wait_ge(z_later, later_before(i - 2))
                col = TILES[i][3]
                v.tensor_scalar(soft[:, i % 4, col:], ring[i % 4 // 2][:, HALF * (i % 2) + col:HALF * (i % 2) + HALF], CAP, None, ALU.min).then_inc(z_capped, 1)
            i = s - 1
            if 0 <= i < len(TILES):
                dve.wait_ge(z_logged, i + 1)
                col = TILES[i][3]
                v.tensor_tensor(soft[:, i % 4, col:], ring[i % 4 // 2][:, HALF * (i % 2) + col:HALF * (i % 2) + HALF], soft[:, i % 4, col:], ALU.max).then_inc(z_soft, 1)
            i = s - 2
            if 0 <= i < len(TILES) and not LAST[i]:
                col = TILES[i][3]
                dve.wait_ge(z_soft, i + 1)
                if DIAGONAL[i]:
                    dve.wait_ge(z_soft_cut, sum(DIAGONAL[:i]) + 1)
                if i >= 1:
                    dve.wait_ge(z_summed, i)
                old, new, x_ = later[:, i % 2], later[:, (i + 1) % 2], soft[:, i % 4]
                if later_before(i) > 0:
                    dve.wait_ge(z_later, later_before(i))
                if FIRST[i]:
                    v.tensor_copy(new[:, col:], x_[:, col:]).then_inc(z_later, 1)
                else:
                    before = TILES[i - 1][3]
                    if before > col:
                        v.tensor_copy(new[:, col:before], x_[:, col:before])
                    v.tensor_tensor(new[:, before:], old[:, before:], x_[:, before:], ALU.add).then_inc(z_later, 1)

        def branch(m, f, src, source):
            dve.wait_ge(slot_free, N1 + m + 1)
            v.tensor_tensor(src[:, f], src[:, f], tmp[:], ALU.mult).then_inc(branched, 1)
            dve.wait_ge(branched, (f + 1) if source == ATT else 4 + f + 1)
            low_part2(branch_lo[:, f], branch_hi[:, f], src[:, f], source + f)

        dve.wait_ge(z_taken, 16)
        for f in range(4):
            branch(Z_ATT + f, f, att2, ATT)
            convolve(6)

        at_ln = 0

        def ln_settled(wait=True):
            nonlocal at_ln
            at_ln += 1
            if wait:
                dve.wait_ge(ln_step, at_ln)

        def centre(src, chunks, width, n):
            dve.wait_ge(ln_summed, n)
            v.tensor_scalar(spare[:], aux[1][:], 1.0 / width, None, ALU.mult).then_inc(ln_step, 1)
            ln_settled()
            for k in range(chunks):
                v.tensor_tensor(src[:, k], src[:, k], spare[:], ALU.subtract).then_inc(ln_step, 1)
                ln_settled(k == chunks - 1)

        def add_ln_squares(chunks, first, squares):
            for k in range(chunks):
                dve.wait_ge(ln_squared, squares + k + 1)
                if k == 0:
                    v.tensor_copy(stat_sum[:], aux[1][:]).then_inc(ln_step, 1)
                    ln_settled()
                else:
                    v.tensor_tensor(stat_sum[:], aux[1][:], stat_sum[:], ALU.add).then_inc(ln_step, 1)
                    ln_settled()

        for f in range(8):
            m = G_ATT + 2 * f
            dve.wait_ge(slot_free, N1 + m + 1)
            dve.wait_ge(panel_done, N1 + m + 2)
            v.tensor_tensor(merged[:, f], ring[1][:], tmp[:], ALU.mult).then_inc(slot_free, 1)
            if f < 4:
                convolve(4)
            if f == 4:
                assert taken == len(todo)
                dve.wait_ge(convolved, taken)
                v.tensor_tensor(stat_sum[:], conv_out[:, 0], conv_out[:, 1], ALU.add).then_inc(ln_step, 1)
                ln_settled()
                for k in (2, 3):
                    v.tensor_tensor(stat_sum[:], stat_sum[:], conv_out[:, k], ALU.add).then_inc(ln_step, 1)
                    ln_settled()
                assert at_ln == LN_MEAN1
            if f == 6:
                centre(conv_out, 4, 512, 1)
                assert at_ln == LN_CENTRED1 + 3
        add_ln_squares(4, LN_CENTRED1, 0)
        assert at_ln == LN_VAR1

        def invert_deviation(n):
            dve.wait_ge(ln_root, n)
            v.reciprocal(rstd[:], rstd[:]).then_inc(ln_step, 1)
            ln_settled()

        invert_deviation(1)
        for k in range(4):
            v.tensor_tensor(conv_out[:, k], conv_out[:, k], rstd[:], ALU.mult).then_inc(ln_step, 1)
            ln_settled(False)
        assert at_ln == LN_SCALED1 + 3
        for f in range(4):
            dve.wait_ge(ln_silued, f + 1)
            branch(Z_CONV + f, f, conv_out, CONV)
        for f in range(8):
            m = G_CONV + 2 * f
            dve.wait_ge(slot_free, N1 + m + 1)
            dve.wait_ge(panel_done, N1 + m + 2)
            v.scalar_tensor_tensor(tmp[:], ring[1][:], proj_bias[:, f:f + 1], tmp[:], ALU.add, ALU.mult).then_inc(slot_free, 1)
            dve.wait_ge(slot_free, N1 + m + 2)
            v.tensor_tensor(merged[:, f], merged[:, f], tmp[:], ALU.add).then_inc(merging, 1)
        for k in range(KC):
            low_part2(merged_lo[:, k], merged_hi[:, k], merged[:, k], MERGED + k)
        dve.wait_ge(source_ready, S1 + MERGED + 8)
        for f in range(8):
            dve.wait_ge(panel_done, N1 + W_OUT2 + f + 1)
            if f >= 2:
                dve.wait_ge(y_turned, f - 1)
            v.scalar_tensor_tensor(resid[:, f % 2], P_hi[:, f].bitcast(F32), ALPHA, ring[f % 2][:], ALU.mult, ALU.add).then_inc(slot_free, 1)
            dve.wait_ge(slot_free, N1 + W_OUT2 + f + 1)
            v.scalar_tensor_tensor(resid[:, f % 2], P_lo[:, f].bitcast(F32), ALPHA, resid[:, f % 2], ALU.mult, ALU.add).then_inc(resid_done, 1)
        dve.wait_ge(y_turned, KC)
        v.tensor_scalar(neg_mean[:], aux[1][:, 0:8], -1.0 / D, None, ALU.mult).then_inc(y_normed, 1)
        dve.wait_ge(y_normed, 1)
        dve.wait_ge(ln_loaded, 16 * 2)
        dve.wait_ge(y_taken, KC)
        for b in range(9):
            if b < 8:
                v.scalar_tensor_tensor(y_out[:, b], y_tok[:, b], neg_mean[:, b:b + 1], ln_gain[:], ALU.add, ALU.mult).then_inc(y_normed, 1)
            if b >= 1:
                dve.wait_ge(y_root, b)
                v.reciprocal(deviation[:, b - 1:b], deviation[:, b - 1:b]).then_inc(y_normed, 1)
                dve.wait_ge(y_normed, 1 + min(b + 1, 8) + b)
                v.scalar_tensor_tensor(y_out[:, b - 1], y_out[:, b - 1], deviation[:, b - 1:b], ln_shift[:], ALU.mult, ALU.add).then_inc(y_done, 1)

    ctx.close()


_INS = ["x", "p", "positions", "norm1", "w_in", "pool_w", "pool_scale", "w_out", "norm2", "w_up", "w_down", "norm3",
        "w_gate", "w_ple", "final_norm", "w_in_2", "b_in_2", "conv_w_2", "conv_b_2", "conv_ln_g_2", "conv_ln_b_2",
        "w_att_proj_2", "w_conv_proj_2", "b_conv_proj_2", "w_out_2", "ln_g_2", "ln_b_2"]


def rotary_rates():
    rot, half = 16, 8
    inv = np.float32(500000.0) ** (-np.arange(0, rot, 2, dtype=np.float32) / np.float32(rot))
    r = np.zeros((2, 64), np.float32)
    r[:, 0:half], r[:, half:rot] = -inv, inv
    return r.reshape(P, 1)


def kernel(**inputs):
    import concourse.bacc as bacc
    from concourse.bass_utils import run_bass_kernel_spmd

    nc = bacc.Bacc("TRN2", target_bir_lowering=False, num_devices=1)
    arrays, args = {}, []
    for name in _INS:
        a = np.ascontiguousarray(inputs[name])
        arrays[f"in_{name}"] = a
        args.append(nc.dram_tensor(f"in_{name}", a.shape, mybir.dt.from_np(a.dtype), kind="ExternalInput").ap())
    arrays["rates"] = rotary_rates()
    args.append(nc.dram_tensor("rates", (P, 1), F32, kind="ExternalInput").ap())
    out = nc.dram_tensor("out", (1, S, P * KC), F32, kind="ExternalOutput").ap()
    two_blocks(nc, *args, out)
    r = run_bass_kernel_spmd(nc, [arrays], core_ids=[0])
    return r.results[0]["out"]
```
